# Optimizing a Trainium2 kernel written in Bass

```python
import jax, jax.numpy as jnp
from jax import lax
import numpy as np

D_MODEL = 2048
BATCH = 1
SEQ = 512
DEPTH = 1
DEC_BATCH = 8
DEC_SEQ = 1
PAST_LEN = 2048
PAGE_SIZE = 128

N_META = 16
MIX_DIM = D_MODEL
CONV_DIM = MIX_DIM // 2
CONV_W = 3
HEAD_DIM = 64
ATTN_DIM = MIX_DIM - CONV_DIM
N_HEADS = ATTN_DIM // HEAD_DIM
N_KV_HEADS = 4
GROUP = N_HEADS // N_KV_HEADS
KV_DIM = N_KV_HEADS * HEAD_DIM
WINDOW = 128
BLOCK = WINDOW
ROPE_THETA = 10000.0
D_FF = ((8 * D_MODEL + 767) // 768) * 256
RMS_EPS = 1e-6
NEG_INF = -1e30
IN_COLS = 3 * CONV_DIM + ATTN_DIM + 2 * KV_DIM
SPLIT_POINTS = (CONV_DIM, 2 * CONV_DIM, 3 * CONV_DIM, 3 * CONV_DIM + ATTN_DIM, 3 * CONV_DIM + ATTN_DIM + KV_DIM)

kernel_name = "hymba_conv_swa_sink_decoder_step"

def rms_norm(x, g):
    x32 = x.astype(jnp.float32)
    y = x32 * lax.rsqrt(jnp.mean(x32 * x32, axis=-1, keepdims=True) + RMS_EPS)
    return (y * g.astype(jnp.float32)).astype(x.dtype)

def rope(x, pos):
    half = HEAD_DIM // 2
    inv = ROPE_THETA ** (-jnp.arange(half, dtype=jnp.float32) / half)
    ang = pos.astype(jnp.float32)[:, None] * inv[None, :]
    cos = jnp.cos(ang)[:, None, :]
    sin = jnp.sin(ang)[:, None, :]
    x32 = x.astype(jnp.float32)
    x1, x2 = x32[..., :half], x32[..., half:]
    return jnp.concatenate([x1 * cos - x2 * sin, x2 * cos + x1 * sin], axis=-1).astype(x.dtype)

def project(hn, w_in):
    n, t, _ = hn.shape
    z = hn @ w_in
    b_gate, c_gate, xc, q, k, v = jnp.split(z, SPLIT_POINTS, axis=-1)
    q = q.reshape(n, t, N_HEADS, HEAD_DIM)
    k = k.reshape(n, t, N_KV_HEADS, HEAD_DIM)
    v = v.reshape(n, t, N_KV_HEADS, HEAD_DIM)
    return b_gate, c_gate, xc, q, k, v

def short_conv(u_ext, w):
    t = u_ext.shape[1] - (CONV_W - 1)
    return sum(w[j] * u_ext[:, j:j + t] for j in range(CONV_W))

def sink_softmax(s, mask, sinks):
    sink = sinks.astype(jnp.float32).reshape(N_KV_HEADS, GROUP, 1, 1)
    s = jnp.where(mask, s, NEG_INF)
    m = jnp.maximum(jnp.max(s, axis=-1, keepdims=True), sink)
    p = jnp.exp(s - m)
    denom = jnp.sum(p, axis=-1, keepdims=True) + jnp.exp(sink - m)
    return p / denom

def attn_prompt(q, k, v, sinks):
    b, l = q.shape[0], q.shape[1]
    pad = BLOCK - N_META
    nb = (l + pad) // BLOCK
    qb = jnp.pad(q, ((0, 0), (pad, 0), (0, 0), (0, 0))).reshape(b, nb, BLOCK, N_KV_HEADS, GROUP, HEAD_DIM)
    kp = jnp.pad(k, ((0, 0), (pad + BLOCK, 0), (0, 0), (0, 0))).reshape(b, nb + 1, BLOCK, N_KV_HEADS, HEAD_DIM)
    vp = jnp.pad(v, ((0, 0), (pad + BLOCK, 0), (0, 0), (0, 0))).reshape(b, nb + 1, BLOCK, N_KV_HEADS, HEAD_DIM)
    kb = jnp.concatenate([kp[:, :-1], kp[:, 1:]], axis=2)
    vb = jnp.concatenate([vp[:, :-1], vp[:, 1:]], axis=2)
    s = jnp.einsum('bnqkgd,bnskd->bnkgqs', qb, kb, preferred_element_type=jnp.float32) * (HEAD_DIM ** -0.5)
    blk = jnp.arange(nb)[:, None, None]
    qi = jnp.arange(BLOCK)[None, :, None]
    kj = jnp.arange(2 * BLOCK)[None, None, :]
    pos_q = blk * BLOCK + qi - pad
    pos_k = blk * BLOCK + kj - BLOCK - pad
    diff = pos_q - pos_k
    mask = ((pos_k >= 0) & (diff >= 0) & (diff <= WINDOW))[:, None, None]
    p = sink_softmax(s, mask, sinks)
    o = jnp.einsum('bnkgqs,bnskd->bnqkgd', p.astype(v.dtype), vb)
    return o.reshape(b, nb * BLOCK, ATTN_DIM)[:, pad:]

def attn_sample(q, k_all, v_all, sinks):
    n, t = q.shape[0], q.shape[1]
    qg = q.reshape(n, t, N_KV_HEADS, GROUP, HEAD_DIM)
    s = jnp.einsum('btkgd,bskd->bkgts', qg, k_all, preferred_element_type=jnp.float32) * (HEAD_DIM ** -0.5)
    pos_q = PAST_LEN + jnp.arange(t)
    pos_k = PAST_LEN - WINDOW + jnp.arange(k_all.shape[1])
    diff = pos_q[:, None] - pos_k[None, :]
    mask = (diff >= 0) & (diff <= WINDOW)
    p = sink_softmax(s, mask, sinks)
    o = jnp.einsum('bkgts,bskd->btkgd', p.astype(v_all.dtype), v_all)
    return o.reshape(n, t, ATTN_DIM)

def merge_groups(b_gate, conv_y, attn_o, conv_g, attn_g, w_out):
    yc = rms_norm(b_gate * conv_y, conv_g)
    ya = rms_norm(attn_o, attn_g)
    return jnp.concatenate([yc, ya], axis=-1) @ w_out

def swiglu(hn, w_gate, w_up, w_down):
    return (jax.nn.silu(hn @ w_gate) * (hn @ w_up)) @ w_down

def setup_inputs(seed: int = 0) -> dict:
    key = jax.random.key(seed)
    ks = jax.random.split(key, 20)
    f32 = jnp.float32
    nrm = lambda k, shape, sc: jax.random.normal(k, shape, f32) * sc
    return {
        "x_prompt": nrm(ks[0], (BATCH, SEQ, D_MODEL), 1.0),
        "x_sample": nrm(ks[1], (DEC_BATCH, DEC_SEQ, D_MODEL), 1.0),
        "cache_k": nrm(ks[2], (DEPTH, DEC_BATCH, WINDOW, N_KV_HEADS, HEAD_DIM), 1.0),
        "cache_v": nrm(ks[3], (DEPTH, DEC_BATCH, WINDOW, N_KV_HEADS, HEAD_DIM), 1.0),
        "state_conv": nrm(ks[4], (DEPTH, DEC_BATCH, CONV_W - 1, CONV_DIM), 1.0),
        "meta_tokens": nrm(ks[5], (N_META, D_MODEL), 1.0),
        "norm1_g": 1.0 + nrm(ks[6], (DEPTH, D_MODEL), 0.02),
        "w_in": nrm(ks[7], (DEPTH, D_MODEL, IN_COLS), D_MODEL ** -0.5),
        "conv_w": nrm(ks[8], (DEPTH, CONV_W, CONV_DIM), CONV_W ** -0.5),
        "conv_norm_g": 1.0 + nrm(ks[9], (DEPTH, CONV_DIM), 0.02),
        "attn_norm_g": 1.0 + nrm(ks[10], (DEPTH, ATTN_DIM), 0.02),
        "attn_sinks": nrm(ks[11], (DEPTH, N_HEADS), 1.0),
        "w_out": nrm(ks[12], (DEPTH, MIX_DIM, D_MODEL), MIX_DIM ** -0.5),
        "norm2_g": 1.0 + nrm(ks[13], (DEPTH, D_MODEL), 0.02),
        "w_gate": nrm(ks[14], (DEPTH, D_MODEL, D_FF), D_MODEL ** -0.5),
        "w_up": nrm(ks[15], (DEPTH, D_MODEL, D_FF), D_MODEL ** -0.5),
        "w_down": nrm(ks[16], (DEPTH, D_FF, D_MODEL), D_FF ** -0.5),
        "final_norm_g": 1.0 + nrm(ks[17], (D_MODEL,), 0.02),
    }

def reference(x_prompt, x_sample, cache_k, cache_v, state_conv, meta_tokens, norm1_g, w_in, conv_w,
              conv_norm_g, attn_norm_g, attn_sinks, w_out, norm2_g, w_gate, w_up, w_down, final_norm_g):
    nbp = x_prompt.shape[0]
    meta = jnp.broadcast_to(meta_tokens[None].astype(x_prompt.dtype), (nbp, N_META, D_MODEL))
    hp = jnp.concatenate([meta, x_prompt], axis=1)
    hs = x_sample
    pos_p = jnp.arange(hp.shape[1])
    pos_s = PAST_LEN + jnp.arange(hs.shape[1])
    nkp, nvp, ncp, nks, nvs, ncs = [], [], [], [], [], []
    for l in range(DEPTH):
        hn = rms_norm(hp, norm1_g[l])
        bg, cg, xc, q, k, v = project(hn, w_in[l])
        u = cg * xc
        cy = short_conv(jnp.pad(u, ((0, 0), (CONV_W - 1, 0), (0, 0))), conv_w[l])
        q = rope(q, pos_p)
        k = rope(k, pos_p)
        ao = attn_prompt(q, k, v, attn_sinks[l])
        hp = hp + merge_groups(bg, cy, ao, conv_norm_g[l], attn_norm_g[l], w_out[l])
        hp = hp + swiglu(rms_norm(hp, norm2_g[l]), w_gate[l], w_up[l], w_down[l])
        nkp.append(k[:, -WINDOW:])
        nvp.append(v[:, -WINDOW:])
        ncp.append(u[:, -(CONV_W - 1):])
        hn = rms_norm(hs, norm1_g[l])
        bg, cg, xc, q, k, v = project(hn, w_in[l])
        u_ext = jnp.concatenate([state_conv[l].astype(hs.dtype), cg * xc], axis=1)
        cy = short_conv(u_ext, conv_w[l])
        q = rope(q, pos_s)
        k = rope(k, pos_s)
        k_all = jnp.concatenate([cache_k[l].astype(k.dtype), k], axis=1)
        v_all = jnp.concatenate([cache_v[l].astype(v.dtype), v], axis=1)
        ao = attn_sample(q, k_all, v_all, attn_sinks[l])
        hs = hs + merge_groups(bg, cy, ao, conv_norm_g[l], attn_norm_g[l], w_out[l])
        hs = hs + swiglu(rms_norm(hs, norm2_g[l]), w_gate[l], w_up[l], w_down[l])
        nks.append(k_all[:, -WINDOW:])
        nvs.append(v_all[:, -WINDOW:])
        ncs.append(u_ext[:, -(CONV_W - 1):])
    y_prompt = rms_norm(hp[:, N_META:], final_norm_g)
    y_sample = rms_norm(hs, final_norm_g)
    return (y_prompt, y_sample, jnp.stack(nkp), jnp.stack(nvp), jnp.stack(ncp),
            jnp.stack(nks), jnp.stack(nvs), jnp.stack(ncs))


_drawn_inputs = setup_inputs


def setup_inputs(seed=0):
    import zlib

    import numpy as np

    out = dict(_drawn_inputs(seed))
    spreads = {}
    factors = {'conv_norm_g': 5.26,
     'attn_norm_g': 5.352,
     'attn_sinks': 6.599,
     'norm2_g': 4.895,
     'final_norm_g': 2.822}
    for name, (base, spread) in spreads.items():
        noise = np.random.default_rng([zlib.crc32(name.encode()), seed]).standard_normal(out[name].shape)
        drawn = base * np.exp(spread * noise) if base else spread * noise
        out[name] = __import__('jax').numpy.asarray(drawn.astype(out[name].dtype))
    for name, factor in factors.items():
        out[name] = (out[name] * factor).astype(out[name].dtype)
    return out
```

```python
from contextlib import ExitStack

import numpy as np

import concourse.bass as bass
import concourse.mybir as mybir

F32 = mybir.dt.float32
F32R = mybir.dt.float32r
ALU = mybir.AluOpType
ACT = mybir.ActivationFunctionType
AX = mybir.AxisListType

P = 128
D_MODEL = 2048
SEQ = 512
NB = 8
N_META = 16
CONV = 1024
HEAD = 64
N_HEADS = 16
N_KV = 4
WINDOW = 128
D_FF = 5632
PAST = 2048
EPS = 1e-6

TOK = N_META + SEQ + NB
OUT = SEQ + NB
SMP = N_META + SEQ
KT = D_MODEL // P
CT = CONV // P
PADK = WINDOW - N_META
PC = PADK + TOK
NWIN = SEQ // P
KCOL = P + 1
FT = 4
NCH = D_FF // P // FT
UNIT = KT * P
HALF = UNIT // 2
W_KV, W_CX, W_OUT = TOK // 2, (TOK - 12) // 2, OUT // 2
CX0 = 12

U_KV, U_P1, U_P2, U_P3 = 0, 4, 36, 52

G1, G2, GCA, CW = 0, 16, 32, 48
N_PAR = 72


class Semaphores:

    def __init__(self, sem):
        self.ident_in = sem("ident_in")
        self.const_in = sem("const_in")
        self.par_in = sem("par_in")
        self.state_in = sem("state_in")
        self.sink_in = sem("sink_in")
        self.kc_in = sem("kc_in")
        self.vc_in = sem("vc_in")
        self.gf_in = sem("gf_in")
        self.xa0 = sem("xa0")
        self.xa1 = sem("xa1")
        self.xa2 = sem("xa2")
        self.xa3 = sem("xa3")
        self.raw00 = sem("raw00")
        self.raw01 = sem("raw01")
        self.raw10 = sem("raw10")
        self.raw11 = sem("raw11")
        self.scr0 = sem("scr0")
        self.scr1 = sem("scr1")
        self.scr2 = sem("scr2")
        self.scr3 = sem("scr3")
        self.xr0 = sem("xr0")
        self.xr1 = sem("xr1")
        self.vout = sem("vout")
        self.kout = sem("kout")
        self.uout = sem("uout")
        self.yout = sem("yout")
        self.shift = sem("shift")
        self.par_turned = sem("par_turned")
        self.par_copied = sem("par_copied")
        self.x_turned = sem("x_turned")
        self.x_copied = sem("x_copied")
        self.x_hi_made = sem("x_hi_made")
        self.a_hi_made = sem("a_hi_made")
        self.a_lo_made = sem("a_lo_made")
        self.hi_made = sem("hi_made")
        self.lo_made = sem("lo_made")
        self.unit_done = sem("unit_done")
        self.free0 = sem("free0")
        self.free1 = sem("free1")
        self.free2 = sem("free2")
        self.free3 = sem("free3")
        self.act_free = sem("act_free")
        self.square_made = sem("square_made")
        self.acc_added = sem("acc_added")
        self.acc_zeroed = sem("acc_zeroed")
        self.ss_done = sem("ss_done")
        self.root_made = sem("root_made")
        self.rstd_made = sem("rstd_made")
        self.rsq_made = sem("rsq_made")
        self.tables_made = sem("tables_made")
        self.v_scaled = sem("v_scaled")
        self.v_sample = sem("v_sample")
        self.pads_zeroed = sem("pads_zeroed")
        self.ones_made = sem("ones_made")
        self.sink8_made = sem("sink8_made")
        self.s_read = sem("s_read")
        self.kv_copied = sem("kv_copied")
        self.rot_made = sem("rot_made")
        self.q_made = sem("q_made")
        self.k_made = sem("k_made")
        self.turned = sem("turned")
        self.pt_copied = sem("pt_copied")
        self.qk_done = sem("qk_done")
        self.soft = sem("soft")
        self.exp_sink = sem("exp_sink")
        self.post = sem("post")
        self.prob_made = sem("prob_made")
        self.o_done = sem("o_done")
        self.o_copied = sem("o_copied")
        self.u_made = sem("u_made")
        self.ucol_made = sem("ucol_made")
        self.c0_made = sem("c0_made")
        self.c1_made = sem("c1_made")
        self.c2_made = sem("c2_made")
        self.y_scaled = sem("y_scaled")
        self.knat_turned = sem("knat_turned")
        self.knat_copied = sem("knat_copied")
        self.kc_turned = sem("kc_turned")
        self.kct_copied = sem("kct_copied")
        self.kct_new = sem("kct_new")
        self.qz_zeroed = sem("qz_zeroed")
        self.qz_made = sem("qz_made")
        self.sqk_done = sem("sqk_done")
        self.ssoft = sem("ssoft")
        self.sexp = sem("sexp")
        self.sexp_sink = sem("sexp_sink")
        self.spost = sem("spost")
        self.st_turned = sem("st_turned")
        self.st_copied = sem("st_copied")
        self.spv_done = sem("spv_done")
        self.new_made = sem("new_made")
        self.ys_made = sem("ys_made")
        self.acc_sq = sem("acc_sq")
        self.acc_b = sem("acc_b")
        self.acc_s = sem("acc_s")
        self.u_turned = sem("u_turned")
        self.u_copied = sem("u_copied")
        self.res_sum = sem("res_sum")
        self.res_made = sem("res_made")
        self.silu_made = sem("silu_made")
        self.silu_scaled = sem("silu_scaled")
        self.f_hi_made = sem("f_hi_made")
        self.f_lo_made = sem("f_lo_made")
        self.down_done = sem("down_done")
        self.y_turned = sem("y_turned")
        self.y_scaled_g = sem("y_scaled_g")
        self.last_squared = sem("last_squared")
        self.ss_col = sem("ss_col")
        self.root_col = sem("root_col")
        self.rstd_col = sem("rstd_col")
        self.y_final = sem("y_final")
        self.y_final_act = sem("y_final_act")
        self.y_final_s = sem("y_final_s")


def build(nc, t):
    ctx = ExitStack()
    with ctx:
        def sb(c, name, shape, dt=F32):
            return c.enter_context(nc.sbuf_tensor(name, shape, dt))

        w_hi = sb(ctx, "w_hi", [P, 2, UNIT], F32R)
        w_lo = sb(ctx, "w_lo", [P, 2, UNIT], F32R)
        w_raw = sb(ctx, "w_raw", [P, 2, UNIT])
        res = sb(ctx, "res", [P, KT, OUT])
        rstd = sb(ctx, "rstd", [P, TOK])
        rstd2 = sb(ctx, "rstd2", [P, TOK])
        acc = sb(ctx, "acc", [P, TOK])
        acc_a = sb(ctx, "acc_a", [P, OUT])
        ident = sb(ctx, "ident", [P, P])
        ones = sb(ctx, "ones", [P, P])
        par = sb(ctx, "par", [P, N_PAR])
        eps = sb(ctx, "eps", [P, 1])
        q_s = sb(ctx, "q_s", [P, 2, OUT])
        xs = sb(ctx, "xs", [P, 2, TOK])
        cvs = sb(ctx, "cvs", [P, 3, 538])
        final_col = sb(ctx, "final_col", [P, 5])
        with ExitStack() as c1:
            kv = sb(c1, "kv", [P, 16 * KCOL + 16 * P])
            k_g = sb(c1, "k_g", [P, PC])
            v_g = sb(c1, "v_g", [P, 5, HEAD])
            cos = sb(c1, "cos", [P, TOK])
            sin = sb(c1, "sin", [P, TOK])
            mask = sb(c1, "mask", [P, 2, 256])
            p_pt = sb(c1, "p_pt", [P, 2, 1024])
            st = sb(c1, "st", [P, P])
            ucol = sb(c1, "ucol", [P, CT, 18])
            k_smp = sb(c1, "k_smp", [P, 2, NB])
            v_smp = sb(c1, "v_smp", [P, 2, NB])
            q_smp = sb(c1, "q_smp", [P, 8, NB])
            sink = sb(c1, "sink", [P, N_HEADS])
            sink8 = sb(c1, "sink8", [P, N_HEADS])
            sinkc = sb(c1, "sinkc", [P, 2])
            stat = sb(c1, "stat", [P, 6, 4])
            sst = sb(c1, "sst", [P, 6])
            a_hi = sb(c1, "a_hi", [P, KT, TOK], F32R)
            a_lo = sb(c1, "a_lo", [P, KT, TOK], F32R)
        SHARED = (16 * KCOL + 16 * P) + PC + 5 * HEAD + 2 * TOK + 512 + 2048 + P + CT * 18
        with ExitStack() as c2:
            f_hi = sb(c2, "f_hi", [P, FT, OUT], F32R)
            f_lo = sb(c2, "f_lo", [P, FT, OUT], F32R)
            g_fin = sb(c2, "g_fin", [P, D_MODEL])
            y_s = sb(c2, "y_s", [NB, D_MODEL])
            pad = SHARED - 2 * FT * OUT - 2 * D_MODEL
            sb(c2, "pad", [P, pad])
            y_nat = sb(c2, "y_nat", [P, NWIN, D_MODEL])

        kd = kv[:, 0:N_KV * PC].rearrange("p (g c) -> p g c", g=N_KV)
        v_nat = kv[:, N_KV * PC:N_KV * PC + 5 * 256].rearrange("p (b d) -> p b d", b=5)
        kc_t = kv[:, 0:16 * KCOL].rearrange("p (x c) -> p x c", x=16)
        cache = kv[:, 16 * KCOL:].rearrange("p (b d) -> p b d", b=NB)
        x_nat = res[:, :, :].rearrange("p k n -> p (k n)")[:, 0:4 * D_MODEL].rearrange("p (t f) -> p t f", t=4)
        x_tail = p_pt[:, :, :].rearrange("p a b -> p (a b)")
        prob = p_pt[:, 0, :].rearrange("p (h k) -> p h k", h=4)
        p_t = p_pt[:, 1, :].rearrange("p (a n) -> p a n", a=2)
        vs8 = p_pt[0:NB, 1, 512:768]
        k_nat = p_pt[:, 1, 0:256]
        k_nat8 = p_pt[0:NB, 1, 256:512]
        u_out = p_pt[0:18, 0, :]
        v_t = cvs[:, :, :].rearrange("p a b -> p (a b)")[:, 0:2 * PC].rearrange("p (t c) -> p t c", t=2)
        par_nat = cvs[:, 0, 0:P]
        st_nat = cvs[:, 0, P:2 * P]
        x_ring = [xs[:, 0, :], xs[:, 1, :], cvs[:, 1, 0:TOK], cvs[:, 2, 0:TOK]]
        squares = [k_g[:, 0:TOK], q_s[:, :, :].rearrange("p a n -> p (a n)")[:, 0:TOK]]
        cx, u_buf, cy = cvs[:, 0, :], cvs[:, 1, :], cvs[:, 2, :]
        rot, zc = xs[:, 0, :], xs[:, 1, :]
        qz = xs[:, 0, 0:512].rearrange("p (x c) -> p x c", x=16)
        ps_s = xs[:, 1, 0:KCOL]
        pt_s = xs[:, 1, 130:130 + 256]
        nv_s = xs[:, 1, 400:528].rearrange("p (t b h) -> p t b h", t=2, b=NB)
        x_res = q_s
        t_c, t_a = xs[:, 0, 0:OUT], xs[:, 1, 0:OUT]

        pu = [ctx.enter_context(nc.psum_tensor(f"pu{i}", [P, 2, 512], F32)) for i in range(2)]
        pa = ctx.enter_context(nc.psum_tensor("pa", [P, 4, 512], F32))
        flat = pa[:, :, :].rearrange("p a b -> p (a b)")
        par_ps, st_ps = pu[0][:, 0, 0:N_PAR], pu[1][:, 1, 0:P]
        s_ps = flat[:, 0:1024].rearrange("p (h k) -> p h k", h=4)
        pair = [pu[0][:, :, :], pu[1][:, :, :], pa[:, 0:2, :], pa[:, 2:4, :]]

        s = Semaphores(lambda name: ctx.enter_context(nc.semaphore(name)))
        raw_in = [[s.raw00, s.raw01], [s.raw10, s.raw11]]
        free = [s.free0, s.free1, s.free2, s.free3]
        x_in, scr_out, xr_in = [s.xa0, s.xa1, s.xa2, s.xa3], [s.scr0, s.scr1, s.scr2, s.scr3], [s.xr0, s.xr1]

        ORDER2 = [0, 1, 2, 3, 4, 5, 6] + list(range(8, 16)) + [7]

        block = ctx.enter_context(nc.Block())

        win = t["w_in"][0].rearrange("(k p) (c n) -> c p k n", p=P, n=P)
        wout = t["w_out"][0].rearrange("(k p) (c n) -> c p k n", p=P, n=P)
        wgate = t["w_gate"][0].rearrange("(k p) (c n) -> c p k n", p=P, n=P)
        wup = t["w_up"][0].rearrange("(k p) (c n) -> c p k n", p=P, n=P)
        wdown = t["w_down"][0].rearrange("(c k p) (d n) -> c d p k n", k=FT, p=P, n=512)
        C_B, C_C, C_X, C_Q, C_K, C_V = 0, 8, 16, 24, 32, 34

        @block.sync
        def _(sp):
            def load_x(c):
                f = slice(512 * c, 512 * c + 512)
                if c == 0:
                    sp.dma_start(x_nat[0:N_META, 0, :], t["meta_tokens"][:, :]).then_inc(x_in[0], 16)
                    sp.dma_start(x_tail[0:16, :], t["x_prompt"][0, 496:512, :]).then_inc(x_in[0], 16)
                    sp.dma_start(x_tail[16:24, :], t["x_sample"][:, 0, :]).then_inc(x_in[0], 16)
                sp.dma_start(x_nat[N_META:P, 0, f], t["x_prompt"][0, 0:PADK, f]).then_inc(x_in[c], 16)
                sp.dma_start(x_nat[:, 1:4, f], t["x_prompt"][0, PADK:PADK + 384, f].rearrange(
                    "(t p) f -> p t f", p=P)).then_inc(x_in[c], 16)

            def load(m, slot, src, first=False, down=False, parts=(0, 1), second=False):
                for h in parts:
                    if second:
                        sp.wait_ge(s.lo_made, 2 * h + slot + 1)
                    elif not first:
                        sp.wait_ge(s.lo_made, 4 * m + 2 * slot + h - 3)
                    dst = w_raw[:, slot, h * HALF:(h + 1) * HALF]
                    if down:
                        sp.dma_start(dst.rearrange("p (k n) -> p k n", n=512),
                                     src[:, 2 * h:2 * h + 2, :]).then_inc(raw_in[slot][h], 16)
                    else:
                        sp.dma_start(dst.rearrange("p (k n) -> p k n", n=P),
                                     src[:, 8 * h:8 * h + 8, :]).then_inc(raw_in[slot][h], 16)

            load_x(0)
            for h in range(2):
                for slot in range(2):
                    load(0, slot, win[C_V + slot], first=True, parts=(h,))
                if h == 0:
                    load_x(1)
            for c in (2, 3):
                sp.wait_ge(s.x_copied, 4 * c - 5)
                load_x(c)
            load(1, 0, win[C_K], second=True)
            load(1, 1, win[C_K + 1], second=True)
            with sp.Fori(0, 4) as g:
                tiles = [C_Q + 2 * g, C_Q + 1 + 2 * g]
                for jj in range(2):
                    tiles += [C_C + jj + 2 * g, C_X + jj + 2 * g, C_B + jj + 2 * g]
                for n in range(8):
                    load(4 * g + (U_P1 + n) // 2, n % 2, win[tiles[n]])
            with sp.Fori(0, 8) as cc:
                for slot in range(2):
                    load(cc + U_P2 // 2, slot, wout[2 * cc + slot])
            with sp.Fori(0, NCH) as c:
                with sp.Fori(0, FT) as f:
                    load(6 * c + f + U_P3 // 2, 0, wgate[4 * c + f])
                    load(6 * c + f + U_P3 // 2, 1, wup[4 * c + f])
                for d in range(4):
                    load(6 * c + U_P3 // 2 + 4 + d // 2, d % 2, wdown[c, d], down=True)
            for b in range(NWIN):
                for h in range(2):
                    if b < 3:
                        sp.wait_ge(s.y_final, 2 * b + h + 1)
                    elif h == 0:
                        sp.wait_ge(s.y_final_act, 1)
                    f = slice(1024 * h, 1024 * h + 1024)
                    sp.dma_start(t["y_prompt"][0, P * b:P * b + P, f], y_nat[:, b, f]).then_inc(s.yout, 16)
            sp.wait_ge(s.y_final_s, 1)
            sp.dma_start(t["y_sample"][:, 0, :], y_s[:, :]).then_inc(s.yout, 16)
            sp.wait_ge(s.yout, 16 * 9)

        @block.tensor
        def _(pe):
            mm = nc.tensor.matmul

            def unit(m, slot, col0, n, inserts=None, ready=None, order=None, tell=False, split=False):
                order = order or range(KT)
                for pos, k in enumerate(order):
                    if inserts and pos in inserts:
                        inserts[pos]()
                    if pos == 0:
                        pe.wait_ge(s.lo_made, 4 * m + 2 * slot + 1)
                    if pos == 8 or (pos < 8 and k >= 8 and order[pos - 1] < 8):
                        pe.wait_ge(s.lo_made, 4 * m + 2 * slot + 2)
                    if ready:
                        pe.wait_ge(s.a_lo_made, ready + pos)
                    if split:
                        outs = pu[slot] if k < 8 else pa[:, 2 * slot:2 * slot + 2, :]
                        start, stop = k in (0, 8), k in (7, 15)
                        outs = [outs[:, h, 0:n] for h in range(2)]
                    else:
                        outs = [pu[slot][:, h, 0:n] for h in range(2)]
                        start, stop = pos == 0, pos == KT - 1
                    w = slice(k * P, k * P + P)
                    passes = [(w_hi, a_hi), (w_hi, a_lo), (w_lo, a_hi)]
                    for i, (wt, a) in enumerate(passes):
                        for h in range(2):
                            last = mm(outs[h], wt[:, slot, w], a[:, k, col0 + h * n:col0 + h * n + n],
                                      start=start and i == 0, stop=stop and i == 2)
                    if tell and pos < KT - 1:
                        last.then_inc(s.act_free, 1)
                last.then_inc(s.unit_done, 1)

            pe.wait_ge(s.ident_in, 16)
            pe.wait_ge(s.par_in, 5 * 16)
            pe.transpose(par_ps, par_nat[0:N_PAR, :], ident[0:N_PAR, 0:N_PAR]).then_inc(s.par_turned, 1)

            def turn_x(k):
                if k % 4 == 0:
                    pe.wait_ge(x_in[k // 4], (5 if k == 0 else 2) * 16)
                if k >= 2:
                    pe.wait_ge(s.x_copied, k - 1)
                o = flat[:, 1024 * (k % 2):1024 * (k % 2) + TOK]
                for b in range(4):
                    pe.transpose(o[:, P * b:P * b + P], x_nat[:, b, P * k:P * k + P], ident[:, :])
                pe.transpose(o[:, 512:TOK], x_tail[0:24, P * k:P * k + P],
                             ident[0:24, 0:24]).then_inc(s.x_turned, 1)

            turn_x(0)
            pe.wait_ge(s.state_in, 16)
            pe.transpose(st_ps, st_nat, ident[:, :]).then_inc(s.par_turned, 1)
            turn_x(1)

            def v_part(k, slot, i):
                wt, a = [(w_hi, a_hi), (w_lo, a_hi), (w_hi, a_lo)][i]
                if (i, k) in ((1, 0), (0, 8)):
                    pe.wait_ge(s.lo_made, k // 4 + slot + 1)
                for h in range(2):
                    last = mm(pu[slot][:, h, 0:W_KV], wt[:, slot, k * P:k * P + P],
                              a[:, k, h * W_KV:h * W_KV + W_KV], start=k == 0 and i == 0, stop=k == KT - 1 and i == 2)
                return last

            for k in range(KT):
                if k + 2 < KT:
                    turn_x(k + 2)
                if k == 0:
                    pe.wait_ge(s.x_hi_made, 1)
                    pe.wait_ge(s.par_copied, 2)
                    for slot in range(2):
                        pe.wait_ge(s.hi_made, slot + 1)
                        v_part(k, slot, 0)
                        if slot == 0:
                            pe.wait_ge(s.a_lo_made, 1)
                        v_part(k, slot, 2)
                    for slot in range(2):
                        v_part(k, slot, 1)
                elif k < KT - 3:
                    pe.wait_ge(s.x_hi_made, k + 1)
                    for slot in range(2):
                        v_part(k, slot, 0)
                        v_part(k, slot, 1)
                    pe.wait_ge(s.a_lo_made, k + 1)
                    for slot in range(2):
                        v_part(k, slot, 2)
            for slot in range(2):
                for k in range(KT - 3, KT):
                    pe.wait_ge(s.a_lo_made, k + 1)
                    for i in range(3):
                        last = v_part(k, slot, i)
                last.then_inc(s.unit_done, 1)

            def norm1_sum():
                pe.wait_ge(s.acc_added, 16)
                pe.wait_ge(s.ones_made, 1)
                pe.wait_ge(s.x_copied, 16)
                for h in range(2):
                    last = mm(pa[:, h, 0:W_KV], ones[:, :], acc[:, h * W_KV:h * W_KV + W_KV], start=True, stop=True)
                last.then_inc(s.ss_done, 1)

            def turn_v():
                pe.wait_ge(s.v_scaled, 2)
                pe.wait_ge(s.pads_zeroed, 2)
                pe.wait_ge(s.root_made, 1)
                for b in range(6):
                    n = P if b < 5 else NB
                    for tt in range(2):
                        last = pe.transpose(flat[0:n, 256 * b + P * tt:256 * b + P * tt + P],
                                            v_t[:, tt, P * b:P * b + n], ident[:, :])
                last.then_inc(s.turned, 1)

            pe.wait_ge(s.free0, 1)
            unit(1, 0, 0, W_KV, {4: norm1_sum, 12: turn_v})
            pe.wait_ge(s.free1, 1)
            unit(1, 1, 0, W_KV)

            def scores(g, i):
                pe.wait_ge(s.kv_copied, 2 * g + 2)
                pe.wait_ge(s.q_made, 4 * g + 4)
                pe.wait_ge(s.s_read, 16 * g + 4 * i + 1)
                for hh in range(2):
                    for pr in range(2):
                        r = slice(HEAD * pr, HEAD * pr + HEAD)
                        last = mm(s_ps[:, 2 * pr + hh, :], q_s[r, hh, P * i:P * i + P], k_g[r, P * i:P * i + 256],
                                  start=hh == 0, stop=True, skip_group_check=True)
                last.then_inc(s.qk_done, 1)

            def turn_p(g, i):
                pe.wait_ge(s.prob_made, 4 * g + i + 1)
                pe.wait_ge(s.pt_copied, 4 * g + i + 1)
                for a in range(2):
                    for h in range(4):
                        last = pe.transpose(flat[:, 1024 + 512 * a + P * h:1024 + 512 * a + P * h + P],
                                            prob[:, h, P * a:P * a + P], ident[:, :])
                last.then_inc(s.turned, 1)

            def values(g, i, m, slot):
                pe.wait_ge(s.pt_copied, 4 * g + i + 2)
                pe.wait_ge(free[1 - slot], m + slot)
                o = pu[1 - slot][:, 0, 0:256]
                for pr in range(2):
                    for a in range(2):
                        last = mm(o[HEAD * pr:HEAD * pr + HEAD, :], v_g[:, i + a, :],
                                  p_t[:, a, 256 * pr:256 * pr + 256], start=a == 0, stop=a == 1)
                last.then_inc(s.o_done, 1)

            def knat():
                pe.wait_ge(s.s_read, 16 * 3 + 1)
                for g in range(N_KV):
                    pe.transpose(flat[:, HEAD * g:HEAD * g + HEAD], kd[0:HEAD, g, 512:640], ident[0:HEAD, 0:HEAD])
                for g in range(N_KV):
                    last = pe.transpose(flat[0:NB, 512 + HEAD * g:512 + HEAD * g + HEAD],
                                        kd[0:HEAD, g, 640:648], ident[0:HEAD, 0:HEAD])
                last.then_inc(s.knat_turned, 1)

            def kcache(rnd):
                pe.wait_ge(s.kc_in, 16)
                pe.wait_ge(s.pt_copied, 13)
                if rnd:
                    pe.wait_ge(s.kct_copied, 1)
                for x in range(8):
                    b, tt = 4 * rnd + x // 2, x % 2
                    last = pe.transpose(flat[:, 1024 + P * x:1024 + P * x + P],
                                        cache[:, b, P * tt:P * tt + P], ident[:, :])
                last.then_inc(s.kc_turned, 1)

            def sample_scores(m, slot):
                pe.wait_ge(s.qz_made, 16)
                pe.wait_ge(s.kct_copied, 2)
                pe.wait_ge(s.kct_new, 1)
                pe.wait_ge(free[1 - slot], m + slot)
                o = pu[1 - slot][:, 1, 0:KCOL]
                for b in range(NB):
                    for tt in range(2):
                        r = 32 * (b // 2)
                        last = mm(o[r:r + 32, :], qz[:, 2 * b + tt, :], kc_t[:, 2 * b + tt, :],
                                  start=b % 2 == 0 and tt == 0, stop=b % 2 == 1 and tt == 1)
                last.then_inc(s.sqk_done, 1)

            def sample_turn():
                pe.wait_ge(s.spost, 3)
                pe.wait_ge(s.s_read, 16 * 4 + 1)
                pe.transpose(flat[:, 0:P], ps_s[:, 0:P], ident[:, :])
                mm(flat[:, P:2 * P], ps_s[:, P:P + 1].to_broadcast([P, P]), ident[:, :],
                   start=True, stop=True).then_inc(s.st_turned, 1)

            def sample_values():
                pe.wait_ge(s.st_copied, 1)
                pe.wait_ge(s.vc_in, 16)
                for tt in range(2):
                    for b in range(NB):
                        c = 512 + 64 * tt + 8 * b
                        last = mm(flat[:, c:c + 8], cache[:, b, P * tt:P * tt + P],
                                  pt_s[:, 16 * b + 8 * tt:16 * b + 8 * tt + 8],
                                  start=tt == 0 and b == 0, stop=True, skip_group_check=True)
                last.then_inc(s.spv_done, 1)

            def turn_u():
                pe.wait_ge(s.ucol_made, 16)
                pe.wait_ge(s.pt_copied, 17)
                for j in range(CT):
                    last = pe.transpose(flat[0:18, 1024 + P * j:1024 + P * j + P], ucol[:, j, :], ident[:, :])
                last.then_inc(s.u_turned, 1)

            def mixers(g, last_g=False):
                for n in range(8):
                    m, slot = 4 * g + (U_P1 + n) // 2, n % 2
                    pe.wait_ge(free[slot], m)
                    if n >= 5:
                        pe.wait_ge(s.o_copied, 4 * g + n - 4)
                    if last_g and n == 3:
                        pe.wait_ge(s.knat_copied, 2)
                    if last_g and n == 7:
                        pe.wait_ge(s.sexp, 1)
                    if 3 <= n <= 6:
                        scores(g, n - 3)
                    ins = {}
                    if n >= 4:
                        ins[4] = lambda n=n: turn_p(g, n - 4)
                        ins[12] = lambda n=n, m=m, slot=slot: values(g, n - 4, m, slot)
                    if last_g:
                        if n == 1:
                            ins[8] = knat
                        if n in (2, 3):
                            ins[8] = lambda n=n: kcache(n - 2)
                        if n == 6:
                            ins[2] = lambda m=m, slot=slot: sample_scores(m, slot)
                        if n == 7:
                            ins[2] = sample_turn
                            ins[8] = sample_values
                            ins[15] = turn_u
                    unit(m, slot, CX0 if n in (2, 3, 5, 6) else N_META, W_CX if n in (2, 3, 5, 6) else W_OUT,
                         ins, tell=last_g and n == 7)
                pe.wait_ge(s.o_copied, 4 * g + 4)

            with pe.Fori(0, 3) as g:
                mixers(g)
            mixers(3, last_g=True)

            def norm_cols(src, outs):
                for h in range(2):
                    last = mm(outs[:, h, 0:W_OUT], ones[:, :], src[:, h * W_OUT:h * W_OUT + W_OUT],
                              start=True, stop=True)
                last.then_inc(s.ss_done, 1)

            def norm_mixers():
                pe.wait_ge(s.acc_added, 24)
                pe.wait_ge(s.free1, 18)
                norm_cols(acc, pu[1])
                pe.wait_ge(s.acc_b, 8)
                pe.wait_ge(s.acc_s, 1)
                pe.wait_ge(s.u_copied, 1)
                norm_cols(acc_a, pa[:, 2:4, :])

            def project(cc, first=False, final=False):
                for slot in range(2):
                    m = cc + U_P2 // 2
                    pe.wait_ge(free[slot], m)
                    if first and slot == 0:
                        pe.wait_ge(s.ys_made, 8)
                        unit(m, slot, N_META, W_OUT, {12: norm_mixers}, ready=17, order=ORDER2, split=True)
                    else:
                        if first:
                            pe.wait_ge(s.root_made, 3)
                        unit(m, slot, N_META, W_OUT, split=True, tell=final and slot == 1)

            project(0, first=True)
            with pe.Fori(1, 7) as cc:
                project(cc)
            project(7, final=True)

            def norm_ffn():
                pe.wait_ge(s.acc_added, 40)
                pe.wait_ge(s.free1, 26)
                norm_cols(acc, pu[1])

            def gate_up(c, f, first=False):
                m = 6 * c + f + U_P3 // 2
                pe.wait_ge(s.free0, 8 * c + f + 26)
                unit(m, 0, N_META, W_OUT, {12: norm_ffn} if first else None, ready=33 if first else None)
                pe.wait_ge(s.free1, 8 * c + f + 26)
                if first:
                    pe.wait_ge(s.root_made, 4)
                unit(m, 1, N_META, W_OUT)

            def down_tile(c, d, o, q, ks=range(FT)):
                slot = d % 2
                for k in ks:
                    if d == 0 and o == 0:
                        pe.wait_ge(s.f_lo_made, 4 * c + k + 1)
                    for i, (wt, a) in enumerate([(w_hi, f_hi), (w_hi, f_lo), (w_lo, f_hi)]):
                        for h in range(2):
                            last = mm(pair[q][:, h, 0:W_OUT], wt[:, slot, 512 * k + P * o:512 * k + P * o + P],
                                      a[:, k, h * W_OUT:h * W_OUT + W_OUT],
                                      start=k == 0 and i == 0, stop=k == FT - 1 and i == 2)
                if o == 3:
                    last.then_inc(s.unit_done, 1)
                elif ks[-1] == FT - 1:
                    last.then_inc(s.down_done, 1)

            def down_start(c):
                for ks in (range(FT - 1), range(FT - 1, FT)):
                    for o in range(2):
                        if ks[0] == 0:
                            pe.wait_ge(free[o], 8 * c + 30)
                        down_tile(c, 0, o, o, ks)

            def down(c):
                for d in range(4):
                    pe.wait_ge(s.lo_made, 2 * (12 * c + U_P3 + 8 + d) + 2)
                    if d == 0:
                        down_start(c)
                    for o in range(2 if d == 0 else 0, 4):
                        if o < 2:
                            pe.wait_ge(free[o], 8 * c + d + 30)
                        elif isinstance(c, int) and c == 0 and d == 0:
                            pass
                        else:
                            pe.wait_ge(free[o], 4 * c + d)
                        down_tile(c, d, o, o)

            gate_up(0, 0, first=True)
            with pe.Fori(1, FT) as f:
                gate_up(0, f)
            down(0)
            with pe.Fori(1, NCH - 1) as c:
                with pe.Fori(0, FT) as f:
                    gate_up(c, f)
                down(c)
            c = NCH - 1
            with pe.Fori(0, FT) as f:
                gate_up(c, f)

            def turn_y(x):
                pe.wait_ge(free[x % 2], 8 * c + 31 + x // 2)
                if x < 2:
                    pe.wait_ge(free[2 + x % 2], 4 * c)
                else:
                    pe.wait_ge(s.y_scaled_g, 2 * (x - 1))
                o = flat[:, 1024 * (x % 2):1024 * (x % 2) + 640]
                for b in range(NWIN):
                    pe.transpose(o[:, P * b:P * b + P], res[:, x, P * b:P * b + P], ident[:, :])
                pe.transpose(o[0:NB, 512:640], res[:, x, SEQ:OUT], ident[:, :]).then_inc(s.y_turned, 1)

            for x in range(KT):
                d, o = x // 4, x % 4
                if o == 0:
                    pe.wait_ge(s.lo_made, 2 * (12 * c + U_P3 + 8 + d) + 2)
                if x == 0:
                    down_start(c)
                elif x > 1:
                    pe.wait_ge(free[x % 2], 8 * c + 30 + x // 2)
                    down_tile(c, d, o, x % 2)
                if x >= 1:
                    turn_y(x - 1)
            turn_y(KT - 1)
            for i, (sq, done, n_sq) in enumerate([(acc, s.acc_added, 55), (u_buf, s.last_squared, 1)]):
                pe.wait_ge(done, n_sq)
                for b in range(5):
                    n = P if b < 4 else NB
                    last = mm(pu[0][0:n, 0, b:b + 1], sq[:, P * b:P * b + n], ones[:, 0:1],
                              start=i == 0 and b == 0, stop=True, skip_group_check=True)
            last.then_inc(s.ss_col, 1)

        def halves(ap):
            return ap.rearrange("p (a n) -> p a n", a=2)

        def heads(ap):
            return ap.rearrange("p (hh q) -> p hh q", hh=2)

        @block.scalar
        def _(act):
            def weights(m, slot, first=False):
                if not first:
                    act.wait_ge(s.unit_done, 2 * m + slot - 1)
                for h in range(2):
                    part = slice(h * HALF, h * HALF + HALF)
                    act.wait_ge(raw_in[slot][h], 16 * m + 16)
                    act.activation(w_hi[:, slot, part], w_raw[:, slot, part], ACT.Copy).then_inc(s.hi_made, 1)

            act.dma_start(ident[:, :], t["c_ident"]).then_inc(s.ident_in, 16)
            act.dma_start(par_nat[0:16, :], t["norm1_g"][0].rearrange("(k p) -> k p", p=P)).then_inc(s.par_in, 16)
            act.dma_start(par_nat[16:32, :], t["norm2_g"][0].rearrange("(k p) -> k p", p=P)).then_inc(s.par_in, 16)
            act.dma_start(par_nat[32:40, :], t["conv_norm_g"][0].rearrange("(k p) -> k p", p=P)).then_inc(s.par_in, 16)
            act.dma_start(par_nat[40:48, :], t["attn_norm_g"][0].rearrange("(k p) -> k p", p=P)).then_inc(s.par_in, 16)
            act.dma_start(par_nat[48:72, :], t["conv_w"][0].rearrange("w (j p) -> (w j) p", p=P)).then_inc(s.par_in, 16)
            act.dma_start(st_nat, t["state_conv"][0].rearrange("b s (j p) -> (b s j) p", p=P)).then_inc(s.state_in, 16)

            def first_hi(slot, h):
                part = slice(h * HALF, h * HALF + HALF)
                act.wait_ge(raw_in[slot][h], 16)
                act.activation(w_hi[:, slot, part], w_raw[:, slot, part], ACT.Copy).then_inc(s.hi_made, 1)

            for k in range(KT):
                act.wait_ge(s.x_turned, k + 1)
                if k >= 4:
                    act.wait_ge(s.a_lo_made, k - 3)
                    act.wait_ge(s.square_made, k - 3)
                    act.wait_ge(scr_out[k % 4], 16 * (k // 4))
                act.activation(x_ring[k % 4], flat[:, 1024 * (k % 2):1024 * (k % 2) + TOK],
                               ACT.Copy).then_inc(s.x_copied, 1)
                if k in (0, 1):
                    first_hi(k, 0)
                if k in (2, 3):
                    first_hi(k - 2, 1)
                act.wait_ge(s.x_copied, k + 1)
                if k >= 2:
                    act.wait_ge(s.acc_added, k - 1)
                act.activation(squares[k % 2], x_ring[k % 4], ACT.Square).then_inc(s.square_made, 1)
                act.dma_start(t["x_t"][k], x_ring[k % 4][:, N_META:TOK]).then_inc(scr_out[k % 4], 16)

            act.wait_ge(s.par_copied, 2)
            act.wait_ge(s.a_lo_made, KT)
            act.wait_ge(s.square_made, KT)
            act.wait_ge(scr_out[2], 16 * 4)
            act.wait_ge(scr_out[3], 16 * 4)
            for tt in range(2):
                weights(1, tt)
                act.activation(halves(v_t[:, tt, PADK:PC]), pu[tt][:, :, 0:W_KV], ACT.Copy).then_inc(free[tt], 1)
            act.wait_ge(s.ss_done, 1)
            act.wait_ge(s.ones_made, 2)
            act.activation(halves(rstd[:, :]), pa[:, 0:2, 0:W_KV], ACT.Sqrt,
                           bias=eps[:, 0:1], scale=1.0 / D_MODEL).then_inc(s.root_made, 1)
            act.wait_ge(s.turned, 1)
            act.activation(v_nat.rearrange("p b d -> p (b d)"), flat[:, 0:1280], ACT.Copy).then_inc(s.s_read, 1)
            act.activation(vs8[:, :], flat[0:NB, 1280:1536], ACT.Copy).then_inc(s.pt_copied, 1)
            act.wait_ge(s.s_read, 1)
            act.dma_start(t["new_v_prompt"][0, 0].rearrange("w g d -> w (g d)"), v_nat[:, 4, :]).then_inc(s.vout, 16)
            act.wait_ge(s.pt_copied, 1)
            act.dma_start(t["new_v_sample"][0, :, WINDOW - 1].rearrange("b g d -> b (g d)"),
                          vs8[:, :]).then_inc(s.vout, 16)
            weights(2, 0)
            weights(2, 1)

            def exps(g, i):
                x = 4 * g + i
                act.wait_ge(s.soft, 5 * x + 5)
                act.wait_ge(s.turned, x + 1)
                for h in range(4):
                    act.activation(prob[:, h, :], s_ps[:, h, :], ACT.Exp, bias=stat[:, 1, h:h + 1],
                                   scale=HEAD ** -0.5, accum_out=stat[:, 3, h:h + 1]).then_inc(s.s_read, 1)
                act.activation(stat[:, 4, :], stat[:, 2, :], ACT.Exp).then_inc(s.exp_sink, 1)

            def split(base, g_col, pos, k):
                if k < KT - 1:
                    act.wait_ge(s.act_free, base // 16 * 15 + k + 1)
                else:
                    act.wait_ge(s.unit_done, U_P2 if base == 0 else U_P3)
                if base == 0 and k == 7:
                    act.wait_ge(s.y_scaled, 16)
                elif base == 0 and k < 7:
                    act.wait_ge(s.y_scaled, 14)
                elif base == 0:
                    act.wait_ge(s.ys_made, 8)
                    act.wait_ge(s.o_copied, 16)
                else:
                    act.wait_ge(s.res_made, k + 1)
                act.activation(a_hi[:, k, N_META:TOK], res[:, k, :], ACT.Copy,
                               scale=par[:, g_col + k:g_col + k + 1]).then_inc(s.a_hi_made, 1)

            def mixers(g, last_g=False):
                for n in range(8):
                    m, slot = 4 * g + (U_P1 + n) // 2, n % 2
                    j = (0 if n < 5 else 1) + 2 * g
                    if not (last_g and n == 7):
                        weights(m + 1, slot)
                    if n in (2, 5):
                        act.wait_ge(s.acc_added, j + 16)
                        if last_g and n == 2:
                            act.wait_ge(s.acc_b, 6)
                        act.activation(halves(cx[:, 0:2 * W_CX]), pu[slot][:, :, 0:W_CX],
                                       ACT.Copy).then_inc(free[slot], 1)
                    if last_g and n == 0:
                        act.wait_ge(s.knat_turned, 1)
                        act.activation(k_nat, flat[:, 0:256], ACT.Copy).then_inc(s.knat_copied, 1)
                        act.activation(k_nat8, flat[0:NB, 512:768], ACT.Copy).then_inc(s.knat_copied, 1)
                        act.wait_ge(s.kv_copied, 8)
                        act.wait_ge(s.vout, 32)
                        act.dma_start(cache, t["cache_k"][0].rearrange("b w g d -> w b (g d)")).then_inc(s.kc_in, 16)
                        act.wait_ge(s.knat_copied, 2)
                        act.dma_start(t["new_k_prompt"][0, 0].rearrange("w g d -> w (g d)"),
                                      k_nat).then_inc(s.kout, 16)
                        act.dma_start(t["new_k_sample"][0, :, WINDOW - 1].rearrange("b g d -> b (g d)"),
                                      k_nat8).then_inc(s.kout, 16)
                    if last_g and n in (1, 2):
                        act.wait_ge(s.kc_turned, n)
                        act.activation(kc_t[:, 8 * (n - 1):8 * (n - 1) + 8, 0:P],
                                       flat[:, 1024:2048].rearrange("p (x c) -> p x c", x=8),
                                       ACT.Copy).then_inc(s.kct_copied, 1)
                        if n == 2:
                            act.dma_start(cache, t["cache_v"][0].rearrange("b w g d -> w b (g d)")
                                          ).then_inc(s.vc_in, 16)
                    if last_g and n == 6:
                        act.wait_ge(s.st_turned, 1)
                        act.activation(pt_s, flat[:, 0:256], ACT.Copy).then_inc(s.st_copied, 1)
                    if 3 <= n <= 6:
                        if last_g and n == 3:
                            act.wait_ge(s.kout, 32)
                        act.wait_ge(s.turned, 4 * g + n - 1)
                        act.activation(p_pt[:, 1, :], flat[:, 1024:2048], ACT.Copy).then_inc(s.pt_copied, 1)
                    if n in (3, 6):
                        act.wait_ge(s.u_made, 3 * j + 3)
                        act.activation(cy[:, 0:TOK], u_buf[:, 0:TOK], ACT.Copy,
                                       scale=par[:, bass.ds(j + CW, 1)]).then_inc(s.c0_made, 1)
                    if 2 <= n <= 5:
                        exps(g, n - 2)
                    if last_g and n == 6:
                        for pos in range(4):
                            split(0, GCA, pos, ORDER2[pos])
                    if 3 <= n <= 6:
                        i = n - 3
                        act.wait_ge(s.o_done, 4 * g + i + 1)
                        act.activation(res[:, bass.ds(2 * g + 8, 2), P * i:P * i + P],
                                       heads(pu[slot][:, 0, 0:256]), ACT.Copy).then_inc(s.o_copied, 1)
                    if last_g and n == 5:
                        act.wait_ge(s.ssoft, 4)
                        act.activation(ps_s, pu[1][:, 1, 0:KCOL], ACT.Exp, bias=sst[:, 1:2], scale=HEAD ** -0.5,
                                       accum_out=sst[:, 3:4]).then_inc(s.sexp, 1)
                        act.activation(sst[:, 4:5], sst[:, 2:3], ACT.Exp).then_inc(s.sexp_sink, 1)

            act.wait_ge(s.vout, 32)
            with act.Fori(0, 3) as g:
                mixers(g)
            mixers(3, last_g=True)

            for pos in range(4, KT):
                split(0, GCA, pos, ORDER2[pos])
                if pos == 5:
                    act.wait_ge(s.u_turned, 1)
                    act.activation(u_out, flat[0:18, 1024:2048], ACT.Copy).then_inc(s.u_copied, 1)
                if pos == 8:
                    weights(U_P2 // 2, 1)
            for i, (dst, src) in enumerate([(rstd, pu[1]), (rstd2, pa[:, 2:4, :])]):
                act.wait_ge(s.ss_done, i + 2)
                act.activation(halves(dst[:, 0:OUT]), src[:, :, 0:W_OUT], ACT.Sqrt,
                               bias=eps[:, 0:1], scale=1.0 / CONV).then_inc(s.root_made, 1)
            act.dma_start(t["new_conv_prompt"][0, 0], u_out[0:2, :]).then_inc(s.uout, 16)
            act.dma_start(t["new_conv_sample"][0].rearrange("b s c -> (b s) c"), u_out[2:18, :]).then_inc(s.uout, 16)

            weights(U_P2 // 2 + 1, 0)
            weights(U_P2 // 2 + 1, 1)
            with act.Fori(1, 7) as cc:
                weights(cc + U_P2 // 2 + 1, 0)
                weights(cc + U_P2 // 2 + 1, 1)
            weights(U_P3 // 2, 0)
            for pos in range(KT):
                if pos == 12:
                    weights(U_P3 // 2, 1)
                split(16, G2, pos, pos)
            act.wait_ge(s.ss_done, 4)
            act.activation(halves(rstd[:, 0:OUT]), pu[1][:, :, 0:W_OUT], ACT.Sqrt,
                           bias=eps[:, 0:1], scale=1.0 / D_MODEL).then_inc(s.root_made, 1)

            def gate_up(c, f):
                m = 6 * c + f + U_P3 // 2
                act.wait_ge(s.free0, 8 * c + f + 27)
                act.activation(t_a, t_c, ACT.Silu).then_inc(s.silu_made, 1)
                weights(m + 1, 0)
                act.wait_ge(s.free1, 8 * c + f + 27)
                act.activation(f_hi[:, bass.ds(f, 1), :].rearrange("p a n -> p (a n)"), t_c,
                               ACT.Copy).then_inc(s.f_hi_made, 1)
                weights(m + 1, 1)

            with act.Fori(0, NCH - 1) as c:
                with act.Fori(0, FT) as f:
                    gate_up(c, f)
                for d in range(4):
                    weights(6 * c + U_P3 // 2 + 5 + d // 2, d % 2)
            c = NCH - 1
            with act.Fori(0, FT) as f:
                gate_up(c, f)
            for d in range(2):
                weights(6 * c + U_P3 // 2 + 5, d)
            act.wait_ge(s.free1, 8 * (NCH - 1) + 38)
            act.activation(u_buf[:, 0:OUT], res[:, KT - 1, :], ACT.Square).then_inc(s.last_squared, 1)
            act.wait_ge(s.ss_col, 1)
            act.activation(final_col[:, 0:4], pu[0][:, 0, 0:4], ACT.Sqrt, bias=eps[:, 0:1],
                           scale=1.0 / D_MODEL).then_inc(s.root_col, 1)
            act.activation(final_col[0:NB, 4:5], pu[0][0:NB, 0, 4:5], ACT.Sqrt, bias=eps[0:NB, 0:1],
                           scale=1.0 / D_MODEL).then_inc(s.root_col, 1)
            act.wait_ge(s.rstd_col, 2)
            act.activation(y_nat[:, 3, :], y_nat[:, 3, :], ACT.Copy,
                           scale=final_col[:, 3:4]).then_inc(s.y_final_act, 1)
            act.wait_ge(s.vout, 32)
            act.wait_ge(s.kout, 32)
            act.wait_ge(s.uout, 32)

        @block.vector
        def _(dve):
            def weights(m, slot):
                for h in range(2):
                    part = slice(h * HALF, h * HALF + HALF)
                    dve.wait_ge(s.hi_made, 4 * m + 2 * slot + h + 1)
                    dve.tensor_tensor(w_lo[:, slot, part], w_raw[:, slot, part],
                                      w_hi[:, slot, part].bitcast(F32), ALU.subtract).then_inc(s.lo_made, 1)

            def first_lo(slot, h):
                part = slice(h * HALF, h * HALF + HALF)
                dve.wait_ge(s.hi_made, 2 * h + slot + 1)
                dve.tensor_tensor(w_lo[:, slot, part], w_raw[:, slot, part],
                                  w_hi[:, slot, part].bitcast(F32), ALU.subtract).then_inc(s.lo_made, 1)

            dve.wait_ge(s.par_turned, 1)
            dve.tensor_copy(par[:, :], par_ps).then_inc(s.par_copied, 1)
            dve.wait_ge(s.par_copied, 1)
            for k in range(KT):
                dve.wait_ge(s.x_copied, k + 1)
                dve.tensor_scalar(a_hi[:, k, :], x_ring[k % 4], par[:, G1 + k:G1 + k + 1], None,
                                  ALU.mult).then_inc(s.x_hi_made, 1)
                dve.wait_ge(s.x_hi_made, k + 1)
                dve.scalar_tensor_tensor(out=a_lo[:, k, :], in0=x_ring[k % 4], scalar=par[:, G1 + k:G1 + k + 1],
                                         in1=a_hi[:, k, :].bitcast(F32), op0=ALU.mult,
                                         op1=ALU.subtract).then_inc(s.a_lo_made, 1)
                if k == 0:
                    dve.wait_ge(s.par_turned, 2)
                    dve.tensor_copy(st[:, :], st_ps).then_inc(s.par_copied, 1)
                    first_lo(0, 0)
                    first_lo(1, 0)
                if k in (3, 4):
                    first_lo(k - 3, 1)
            weights(1, 0)
            weights(1, 1)

            dve.wait_ge(s.root_made, 1)
            dve.reciprocal(rstd[:, :], rstd[:, :]).then_inc(s.rstd_made, 1)
            dve.wait_ge(s.rstd_made, 1)
            for tt in range(2):
                dve.wait_ge(free[tt], 1)
                dve.tensor_tensor(v_t[:, tt, PADK:PC], v_t[:, tt, PADK:PC], rstd[:, :],
                                  ALU.mult).then_inc(s.v_scaled, 1)
            dve.wait_ge(s.const_in, 48)
            dve.tensor_tensor(cos[:, :], cos[:, :], rstd[:, :], ALU.mult).then_inc(s.tables_made, 1)
            dve.tensor_tensor(sin[:, :], sin[:, :], rstd[:, :], ALU.mult).then_inc(s.tables_made, 1)
            dve.tensor_tensor(rstd2[:, :], rstd[:, :], rstd[:, :], ALU.mult).then_inc(s.rsq_made, 1)
            dve.wait_ge(s.v_scaled, 2)
            dve.tensor_copy(v_smp[:, :, :], v_t[:, :, PADK + SMP:PC]).then_inc(s.v_sample, 1)
            dve.wait_ge(s.tables_made, 2)

            def rotate(m, slot, col0, n):
                for r in range(4):
                    a, b = 32 * r, 32 * (r ^ 1)
                    last = dve.tensor_tensor(halves(rot[b:b + 32, 0:2 * n]), pu[slot][a:a + 32, :, 0:n],
                                             halves(sin[a:a + 32, col0:col0 + 2 * n]), ALU.mult)
                last.then_inc(s.rot_made, 1)
                dve.tensor_tensor(halves(zc[:, 0:2 * n]), pu[slot][:, :, 0:n],
                                  halves(cos[:, col0:col0 + 2 * n]), ALU.mult).then_inc(free[slot], 1)
                dve.wait_ge(free[slot], m + 1)

            def rotate_k(tt):
                dve.wait_ge(s.unit_done, 3 + tt)
                rotate(1, tt, 0, W_KV)
                dve.wait_ge(s.rot_made, tt + 1)
                for r in range(2):
                    src = slice(HEAD * r, HEAD * r + HEAD)
                    for o in (0, HEAD):
                        dve.tensor_tensor(kd[o:o + HEAD, 2 * tt + r, PADK:PC], zc[src, 0:TOK], rot[src, 0:TOK],
                                          ALU.add).then_inc(s.k_made, 1)
                dve.tensor_tensor(k_smp[:, tt, :], zc[:, SMP:TOK], rot[:, SMP:TOK], ALU.add).then_inc(s.k_made, 1)

            for i in range(2):
                dve.wait_ge(scr_out[i], 16 * 4)
            dve.wait_ge(s.square_made, 16)
            rotate_k(0)
            weights(2, 0)
            dve.wait_ge(s.k_made, 5)
            rotate_k(1)
            weights(2, 1)
            dve.wait_ge(s.sink_in, 16 * (NB + 1))
            dve.tensor_copy(sink[:, :].rearrange("p (g pr hh) -> p g pr hh", g=N_KV, pr=2),
                            sink8[:, :].rearrange("p (g hh pr) -> p g pr hh", g=N_KV, pr=2)).then_inc(s.sink8_made, 1)
            dve.wait_ge(s.sink8_made, 1)
            dve.tensor_scalar(sink8[:, :], sink[:, :], HEAD ** 0.5, None, ALU.mult).then_inc(s.sink8_made, 1)
            dve.tensor_scalar(sinkc[:, 1:2], sinkc[:, 0:1], HEAD ** 0.5, None, ALU.mult).then_inc(s.sink8_made, 1)
            dve.wait_ge(s.sink8_made, 3)
            dve.wait_ge(s.k_made, 10)

            def soft(g, i):
                x = 4 * g + i
                dve.wait_ge(s.qk_done, x + 1)
                dve.tensor_tensor(s_ps, s_ps, mask[:, min(i, 1):min(i, 1) + 1, :].to_broadcast([P, 4, 256]),
                                  ALU.add).then_inc(s.soft, 1)
                dve.wait_ge(s.soft, 5 * x + 1)
                dve.tensor_reduce(stat[:, 0, :], s_ps, AX.X, ALU.max).then_inc(s.soft, 1)
                dve.wait_ge(s.soft, 5 * x + 2)
                dve.tensor_tensor(stat[:, 0, :], stat[:, 0, :], sink8[:, bass.ds(4 * g, 4)],
                                  ALU.max).then_inc(s.soft, 1)
                dve.wait_ge(s.soft, 5 * x + 3)
                dve.tensor_scalar(stat[:, 1, :], stat[:, 0, :], -HEAD ** -0.5, None, ALU.mult).then_inc(s.soft, 1)
                dve.wait_ge(s.soft, 5 * x + 4)
                dve.tensor_tensor(stat[:, 2, :], stat[:, 1, :], sink[:, bass.ds(4 * g, 4)],
                                  ALU.add).then_inc(s.soft, 1)

            def post(g, i):
                x = 4 * g + i
                dve.wait_ge(s.exp_sink, x + 1)
                dve.tensor_tensor(stat[:, 3, :], stat[:, 3, :], stat[:, 4, :], ALU.add).then_inc(s.post, 1)
                dve.wait_ge(s.post, 2 * x + 1)
                dve.reciprocal(stat[:, 5, :], stat[:, 3, :]).then_inc(s.post, 1)

            def split(base, g_col, pos, k):
                dve.wait_ge(s.a_hi_made, base + pos + 1)
                dve.scalar_tensor_tensor(out=a_lo[:, k, N_META:TOK], in0=res[:, k, :],
                                         scalar=par[:, g_col + k:g_col + k + 1],
                                         in1=a_hi[:, k, N_META:TOK].bitcast(F32), op0=ALU.mult,
                                         op1=ALU.subtract).then_inc(s.a_lo_made, 1)

            def evacuate(g, n, m, slot):
                j = (0 if n < 5 else 1) + 2 * g
                dve.wait_ge(s.unit_done, 2 * m + slot + 1)
                if n < 2:
                    rotate(m, slot, N_META, W_OUT)
                    dve.wait_ge(s.rot_made, 2 * g + n + 3)
                    dve.tensor_tensor(q_s[:, n, :], zc[:, 0:OUT], rot[:, 0:OUT], ALU.add).then_inc(s.q_made, 1)
                    dve.tensor_tensor(q_smp[:, bass.ds(2 * g + n, 1), :].rearrange("p a b -> p (a b)"),
                                      zc[:, SEQ:OUT], rot[:, SEQ:OUT], ALU.add).then_inc(s.q_made, 1)
                    dve.wait_ge(s.q_made, 4 * g + 2 * n + 2)
                if n in (3, 6):
                    dve.wait_ge(free[1 - slot], m + 1 if n == 3 else m)
                    c = halves(cx[:, 0:2 * W_CX])
                    dve.tensor_tensor(c, pu[slot][:, :, 0:W_CX], c, ALU.mult).then_inc(free[slot], 1)
                if n in (4, 7):
                    dve.wait_ge(s.c2_made, j + 1)
                    y = res[:, bass.ds(j, 1), :].rearrange("p a n -> p (a n)")
                    r = SEQ - W_OUT
                    dve.tensor_tensor(y[:, 0:W_OUT], pu[slot][:, 0, 0:W_OUT], cy[:, 0:W_OUT], ALU.mult)
                    dve.tensor_tensor(y[:, W_OUT:SEQ], pu[slot][:, 1, 0:r], cy[:, W_OUT:SEQ], ALU.mult)
                    dve.tensor_tensor(y[:, SEQ:OUT], pu[slot][:, 1, r:W_OUT], cy[:, SEQ + 2:SEQ + 2 + 22:3],
                                      ALU.mult).then_inc(free[slot], 1)

            def taps(j):
                for w, made in ((1, s.c1_made), (2, s.c2_made)):
                    dve.wait_ge(s.c0_made if w == 1 else s.c1_made, j + 1)
                    dve.scalar_tensor_tensor(out=cy[:, 0:TOK], in0=u_buf[:, w:w + TOK],
                                             scalar=par[:, bass.ds(j + CW + 8 * w, 1)], in1=cy[:, 0:TOK],
                                             op0=ALU.mult, op1=ALU.add).then_inc(made, 1)

            def sample_queries():
                dve.wait_ge(s.qz_zeroed, 1)
                q6 = qz.rearrange("p (b2 bb t) c -> p b2 bb t c", bb=2, t=2)
                qs = q_smp[:, :, :].rearrange("p c (b2 bb) -> p bb b2 c", bb=2)
                for gm in range(2):
                    for pr in range(2):
                        for tt in range(2):
                            for bb in range(2):
                                c0 = 16 * bb + 8 * tt + 4 * gm + pr
                                dve.tensor_copy(q6[HEAD * gm:HEAD * gm + HEAD, :, bb, tt, c0:c0 + 3:2],
                                                qs[HEAD * pr:HEAD * pr + HEAD, bb, :, 4 * tt + 2 * gm:4 * tt + 2 * gm + 2]
                                                ).then_inc(s.qz_made, 1)
                dve.wait_ge(s.knat_turned, 1)
                dve.wait_ge(s.kv_copied, 8)
                dve.tensor_copy(kc_t[:, :, P:P + 1].rearrange("p (b t) o -> p b (t o)", t=2),
                                k_smp[:, :, :].rearrange("p t b -> p b t")).then_inc(s.kct_new, 1)

            def sample_soft():
                dve.wait_ge(s.sqk_done, 1)
                dve.tensor_reduce(sst[:, 0:1], pu[1][:, 1, 0:KCOL], AX.X, ALU.max).then_inc(s.ssoft, 1)
                dve.wait_ge(s.ssoft, 1)
                dve.tensor_tensor(sst[:, 0:1], sst[:, 0:1], sinkc[:, 1:2], ALU.max).then_inc(s.ssoft, 1)
                dve.wait_ge(s.ssoft, 2)
                dve.tensor_scalar(sst[:, 1:2], sst[:, 0:1], -HEAD ** -0.5, None, ALU.mult).then_inc(s.ssoft, 1)
                dve.wait_ge(s.ssoft, 3)
                dve.tensor_tensor(sst[:, 2:3], sst[:, 1:2], sinkc[:, 0:1], ALU.add).then_inc(s.ssoft, 1)

            def sample_post():
                dve.wait_ge(s.sexp_sink, 1)
                dve.tensor_tensor(sst[:, 3:4], sst[:, 3:4], sst[:, 4:5], ALU.add).then_inc(s.spost, 1)
                dve.wait_ge(s.spost, 1)
                dve.reciprocal(sst[:, 5:6], sst[:, 3:4]).then_inc(s.spost, 1)
                dve.wait_ge(s.spost, 2)
                dve.tensor_scalar(ps_s, ps_s, sst[:, 5:6], None, ALU.mult).then_inc(s.spost, 1)

            def sample_outputs():
                dve.wait_ge(s.st_copied, 1)
                pn = pt_s[:, P:2 * P].rearrange("p (b t h) -> p t b h", b=NB, t=2)
                for tt in range(2):
                    dve.tensor_tensor(nv_s[:, tt], pn[:, tt],
                                      v_smp[:, tt, :].unsqueeze(2).to_broadcast([P, NB, 8]),
                                      ALU.mult).then_inc(s.new_made, 1)
                dve.wait_ge(s.new_made, 2)
                dve.wait_ge(s.spv_done, 1)
                o = flat[:, 512:640].rearrange("p (t b h) -> p t h b", t=2, b=NB)
                nv = nv_s.rearrange("p t b h -> p t h b")
                for gm in range(2):
                    src = slice(HEAD * gm, HEAD * gm + HEAD)
                    for pr in range(2):
                        for tt in range(2):
                            hs = slice(4 * gm + pr, 4 * gm + pr + 3, 2)
                            c0 = 8 + 4 * tt + 2 * gm
                            dve.tensor_tensor(res[HEAD * pr:HEAD * pr + HEAD, c0:c0 + 2, SEQ:OUT],
                                              o[src, tt, hs, :], nv[src, tt, hs, :], ALU.add).then_inc(s.ys_made, 1)

            def mixers(g, last_g=False):
                for n in range(8):
                    m, slot = 4 * g + (U_P1 + n) // 2, n % 2
                    j = (0 if n < 5 else 1) + 2 * g
                    if 2 <= n <= 5:
                        soft(g, n - 2)
                    if not (last_g and n == 7):
                        weights(m + 1, slot)
                    if not (last_g and n == 7):
                        evacuate(g, n, m, slot)
                    if n in (3, 6):
                        taps(j)
                    if last_g and n == 2:
                        sample_queries()
                    if 2 <= n <= 5:
                        post(g, n - 2)
                    if last_g and n == 5:
                        sample_soft()
                        sample_post()
                    if last_g and n == 6:
                        sample_outputs()

            with dve.Fori(0, 3) as g:
                mixers(g)
            mixers(3, last_g=True)
            for pos in range(KT):
                split(0, GCA, pos, ORDER2[pos])
                if pos == 3:
                    evacuate(3, 7, 17, 1)
                if pos == 8:
                    dve.wait_ge(s.acc_sq, 8)
                    dve.tensor_reduce(acc_a[:, SEQ:OUT], q_smp[:, :, :].rearrange("p c b -> p b c"), AX.X,
                                      ALU.add).then_inc(s.acc_s, 1)
                if pos == 11:
                    weights(U_P2 // 2, 1)
            for i, r in enumerate((rstd, rstd2)):
                dve.wait_ge(s.root_made, i + 2)
                dve.reciprocal(r[:, 0:OUT], r[:, 0:OUT]).then_inc(s.rstd_made, 1)
            dve.wait_ge(s.rstd_made, 3)
            dve.wait_ge(s.ys_made, 8)

            def project(cc, slot, first=False):
                m = cc + U_P2 // 2
                dve.wait_ge(s.unit_done, 2 * m + slot + 1)
                if not first:
                    dve.wait_ge(s.res_made, 2 * cc + slot)
                dve.tensor_tensor(halves(t_c), pu[slot][:, :, 0:W_OUT], halves(rstd[:, 0:OUT]), ALU.mult)
                dve.tensor_tensor(halves(t_a), pa[:, 2 * slot:2 * slot + 2, 0:W_OUT], halves(rstd2[:, 0:OUT]),
                                  ALU.mult).then_inc(free[slot], 1)

            project(0, 0, first=True)
            weights(U_P2 // 2 + 1, 0)
            project(0, 1)
            weights(U_P2 // 2 + 1, 1)
            with dve.Fori(1, 7) as cc:
                for slot in range(2):
                    project(cc, slot)
                    weights(cc + U_P2 // 2 + 1, slot)
            project(7, 0)
            weights(U_P3 // 2, 0)
            for pos in range(KT):
                if pos == 12:
                    project(7, 1)
                    weights(U_P3 // 2, 1)
                split(16, G2, pos, pos)
            dve.wait_ge(s.root_made, 4)
            dve.reciprocal(rstd[:, 0:OUT], rstd[:, 0:OUT]).then_inc(s.rstd_made, 1)
            dve.wait_ge(s.rstd_made, 4)

            def gate_up(c, f):
                m = 6 * c + f + U_P3 // 2
                dve.wait_ge(s.unit_done, 2 * m + 1)
                dve.tensor_tensor(halves(t_c), pu[0][:, :, 0:W_OUT], halves(rstd[:, 0:OUT]),
                                  ALU.mult).then_inc(free[0], 1)
                weights(m + 1, 0)
                dve.wait_ge(s.silu_scaled, 4 * c + f + 1)
                dve.wait_ge(s.unit_done, 2 * m + 2)
                dve.tensor_tensor(halves(t_c), pu[1][:, :, 0:W_OUT], halves(t_a), ALU.mult).then_inc(free[1], 1)
                dve.wait_ge(s.f_hi_made, 4 * c + f + 1)
                dve.tensor_tensor(f_lo[:, bass.ds(f, 1), :].rearrange("p a n -> p (a n)"), t_c,
                                  f_hi[:, bass.ds(f, 1), :].rearrange("p a n -> p (a n)").bitcast(F32),
                                  ALU.subtract).then_inc(s.f_lo_made, 1)
                weights(m + 1, 1)
                dve.wait_ge(s.f_lo_made, 4 * c + f + 1)

            def add(c, d, o, q):
                if o < 3:
                    dve.wait_ge(s.down_done, 12 * c + 3 * d + o + 1)
                else:
                    dve.wait_ge(s.unit_done, 12 * c + U_P3 + 9 + d)
                r = halves(res[:, 4 * d + o, :])
                dve.tensor_tensor(r, pair[q][:, :, 0:W_OUT], r, ALU.add).then_inc(free[q], 1)

            dve.wait_ge(s.res_made, 16)
            with dve.Fori(0, NCH - 1) as c:
                with dve.Fori(0, FT) as f:
                    gate_up(c, f)
                for d in range(4):
                    for o in range(4):
                        add(c, d, o, o)
                    weights(6 * c + U_P3 // 2 + 5 + d // 2, d % 2)
            c = NCH - 1
            with dve.Fori(0, FT) as f:
                gate_up(c, f)
            dve.wait_ge(s.gf_in, 16)
            dve.wait_ge(s.vout, 32)
            dve.wait_ge(s.kout, 32)
            dve.wait_ge(s.uout, 32)

            def scale_y(x):
                dve.wait_ge(s.y_turned, x + 1)
                o = flat[:, 1024 * (x % 2):1024 * (x % 2) + 640]
                f = slice(P * x, P * x + P)
                dve.tensor_tensor(y_nat[:, :, f], o[:, 0:512].rearrange("p (b n) -> p b n", b=NWIN),
                                  g_fin[:, f].unsqueeze(1).to_broadcast([P, NWIN, P]),
                                  ALU.mult).then_inc(s.y_scaled_g, 1)
                dve.tensor_tensor(y_s[:, f], o[0:NB, 512:640], g_fin[0:NB, f], ALU.mult).then_inc(s.y_scaled_g, 1)

            for x in range(KT):
                add(c, x // 4, x % 4, x % 2)
                if x in (3, 7):
                    weights(6 * c + U_P3 // 2 + 5, x // 4)
                if x >= 1:
                    scale_y(x - 1)
            scale_y(KT - 1)
            dve.wait_ge(s.root_col, 2)
            dve.reciprocal(final_col[:, 0:4], final_col[:, 0:4]).then_inc(s.rstd_col, 1)
            dve.reciprocal(final_col[0:NB, 4:5], final_col[0:NB, 4:5]).then_inc(s.rstd_col, 1)
            dve.wait_ge(s.rstd_col, 2)
            dve.wait_ge(s.y_scaled_g, 32)
            for b in range(3):
                for h in range(2):
                    y = y_nat[:, b, 1024 * h:1024 * h + 1024]
                    dve.tensor_scalar(y, y, final_col[:, b:b + 1], None, ALU.mult).then_inc(s.y_final, 1)
            dve.tensor_scalar(y_s[:, :], y_s[:, :], final_col[0:NB, 4:5], None, ALU.mult).then_inc(s.y_final_s, 1)

        @block.gpsimd
        def _(pool):
            def sum_squares(src, n, total):
                pool.tensor_tensor(cx[:, 0:n], src, src, ALU.mult).then_inc(s.square_made, 1)
                pool.wait_ge(s.square_made, total)
                pool.tensor_tensor(acc[:, 0:n], acc[:, 0:n], cx[:, 0:n], ALU.add).then_inc(s.acc_added, 1)
                pool.wait_ge(s.acc_added, total)

            pool.memset(acc[:, :], 0.0).then_inc(s.acc_zeroed, 1)
            pool.memset(ones[:, :], 1.0).then_inc(s.ones_made, 1)
            pool.memset(eps[:, :], EPS).then_inc(s.ones_made, 1)
            pool.memset(kd[:, :, 0:PADK], 0.0).then_inc(s.pads_zeroed, 1)
            pool.wait_ge(s.acc_zeroed, 1)
            tables = [(cos[:, :], t["c_cos"]), (sin[:, :], t["c_sin"]), (mask[:, :, :], t["c_mask"])]
            for k in range(KT):
                pool.wait_ge(s.square_made, k + 1)
                pool.tensor_tensor(acc[:, :], acc[:, :], squares[k % 2], ALU.add).then_inc(s.acc_added, 1)
                if k in (6, 8, 10):
                    dst, src = tables[k // 2 - 3]
                    pool.dma_start(dst, src).then_inc(s.const_in, 16)
                pool.wait_ge(s.acc_added, k + 1)
            pool.wait_ge(s.par_turned, 2)
            pool.wait_ge(s.a_lo_made, KT)
            for i in (2, 3):
                pool.wait_ge(scr_out[i], 16 * 4)
            pool.memset(v_t[:, :, 0:PADK], 0.0).then_inc(s.pads_zeroed, 1)
            pool.dma_start(sink8[:, :], t["attn_sinks"].to_broadcast([P, N_HEADS])).then_inc(s.sink_in, 16)
            for b in range(NB):
                pool.dma_start(sinkc[16 * b:16 * b + 16, 0:1],
                               t["attn_sinks"][0].rearrange("(h o) -> h o", o=1)).then_inc(s.sink_in, 16)
            for name, cached in (("new_k_sample", "cache_k"), ("new_v_sample", "cache_v")):
                pool.dma_start(t[name][0, :, 0:WINDOW - 1].rearrange("b w g d -> b w (g d)"),
                               t[cached][0, :, 1:WINDOW].rearrange("b w g d -> b w (g d)")).then_inc(s.shift, 16)
            pool.wait_ge(s.ss_done, 1)
            pool.memset(acc[:, :], 0.0).then_inc(s.acc_zeroed, 1)
            pool.wait_ge(s.acc_zeroed, 2)
            pool.wait_ge(s.k_made, 10)
            pool.wait_ge(s.s_read, 1)
            pool.wait_ge(s.rsq_made, 1)
            pool.wait_ge(s.v_sample, 1)

            def probs(g, i):
                x = 4 * g + i
                pool.wait_ge(s.post, 2 * x + 2)
                pool.tensor_tensor(prob, prob, stat[:, 5, :].unsqueeze(2).to_broadcast([P, 4, 256]),
                                   ALU.mult).then_inc(s.prob_made, 1)

            def conv_input(j, m, slot):
                u3 = u_buf[:, SEQ + 2:SEQ + 2 + 3 * NB].rearrange("p (b s) -> p b s", s=3)
                pool.wait_ge(free[slot], m + 1)
                pool.tensor_tensor(u_buf[:, 0:SEQ + 2], cx[:, 2:SEQ + 4], rstd2[:, N_META - 2:SMP],
                                   ALU.mult).then_inc(s.u_made, 1)
                pool.tensor_tensor(u3[:, :, 2], cx[:, SEQ + 4:SEQ + 4 + NB], rstd2[:, SMP:TOK],
                                   ALU.mult).then_inc(s.u_made, 1)
                stj = st[:, :].rearrange("p (b s j) -> p j b s", b=NB, s=2)
                pool.tensor_copy(u3[:, :, 0:2], stj[:, bass.ds(j, 1)].rearrange("p o b s -> p (o b) s")
                                 ).then_inc(s.u_made, 1)
                pool.wait_ge(s.u_made, 3 * j + 3)
                pool.tensor_copy(ucol[:, bass.ds(j, 1), 0:2].rearrange("p o n -> p (o n)"),
                                 u_buf[:, SEQ:SEQ + 2]).then_inc(s.ucol_made, 1)
                pool.tensor_copy(ucol[:, bass.ds(j, 1), 2:18].rearrange("p o (b s) -> p (o b) s", s=2),
                                 u3[:, :, 1:3]).then_inc(s.ucol_made, 1)
                pool.wait_ge(s.ucol_made, 2 * j + 2)

            def conv_output(j, m, slot):
                pool.wait_ge(free[slot], m + 1)
                y = res[:, bass.ds(j, 1), :].rearrange("p a n -> p (a n)")
                pool.tensor_tensor(cx[:, 0:OUT], y, rstd[:, N_META:TOK], ALU.mult).then_inc(s.y_scaled, 1)
                pool.wait_ge(s.y_scaled, 2 * j + 1)
                pool.tensor_tensor(u_buf[:, 0:OUT], cx[:, 0:OUT], cx[:, 0:OUT], ALU.mult).then_inc(s.square_made, 1)
                pool.tensor_tensor(y, y, rstd[:, N_META:TOK], ALU.mult).then_inc(s.y_scaled, 1)
                pool.wait_ge(s.square_made, j + 17)
                pool.tensor_tensor(acc[:, 0:OUT], acc[:, 0:OUT], u_buf[:, 0:OUT], ALU.add).then_inc(s.acc_added, 1)
                pool.wait_ge(s.acc_added, j + 17)

            def attn_squares(c, i):
                pool.tensor_tensor(cx[:, 0:SEQ] if i else acc_a[:, 0:SEQ], res[:, c, 0:SEQ], res[:, c, 0:SEQ],
                                   ALU.mult).then_inc(s.acc_sq if i else s.acc_b, 1)
                if i:
                    pool.wait_ge(s.acc_sq, i)
                    pool.tensor_tensor(acc_a[:, 0:SEQ], acc_a[:, 0:SEQ], cx[:, 0:SEQ], ALU.add).then_inc(s.acc_b, 1)
                pool.wait_ge(s.acc_b, i + 1)

            def mixers(g, last_g=False):
                pool.wait_ge(s.unit_done, 8 * g + U_P1)
                pool.tensor_copy(k_g[:, :], kd[:, bass.ds(g, 1), :].rearrange("p o c -> p (o c)")
                                 ).then_inc(s.kv_copied, 1)
                pool.tensor_copy(v_g[:, :, :], v_nat[:, :, bass.ds(HEAD * g, HEAD)]).then_inc(s.kv_copied, 1)
                if last_g:
                    pool.wait_ge(s.o_copied, 12)
                    for i in range(6):
                        attn_squares(8 + i, i)
                    pool.wait_ge(s.q_made, 16)
                    pool.memset(qz, 0.0).then_inc(s.qz_zeroed, 1)
                for n in range(8):
                    m, slot = 4 * g + (U_P1 + n) // 2, n % 2
                    j = (0 if n < 5 else 1) + 2 * g
                    if n in (3, 6):
                        conv_input(j, m, slot)
                    if n == 4 or (n == 7 and not last_g):
                        conv_output(j, m, slot)
                    if 2 <= n <= 5:
                        probs(g, n - 2)

            with pool.Fori(0, 3) as g:
                mixers(g)
            mixers(3, last_g=True)
            for out in scr_out:
                pool.wait_ge(out, 16 * 4)
            for i in range(2):
                pool.dma_start(x_res[:, i, :], t["x_t"][i]).then_inc(xr_in[i], 16)
            pool.wait_ge(s.o_copied, 16)
            attn_squares(14, 6)
            attn_squares(15, 7)
            pool.wait_ge(s.ys_made, 8)
            smp = res[:, 8:16, SEQ:OUT]
            pool.tensor_tensor(q_smp[:, :, :], smp, smp, ALU.mult).then_inc(s.acc_sq, 1)
            conv_output(7, 17, 1)
            pool.wait_ge(s.ss_done, 2)
            pool.memset(acc[:, :], 0.0).then_inc(s.acc_zeroed, 1)
            pool.wait_ge(s.acc_zeroed, 3)

            def project(cc, slot, more=True):
                m = cc + U_P2 // 2
                x = 2 * cc + slot
                pool.wait_ge(free[slot], m + 1)
                pool.tensor_tensor(t_c, t_c, t_a, ALU.add).then_inc(s.res_sum, 1)
                pool.wait_ge(s.res_sum, x + 1)
                pool.wait_ge(xr_in[slot], 16 * cc + 16)
                r = res[:, bass.ds(x, 1), :].rearrange("p a n -> p (a n)")
                pool.tensor_tensor(r, t_c, x_res[:, slot, :], ALU.add).then_inc(s.res_made, 1)
                pool.wait_ge(s.res_made, x + 1)
                if more:
                    pool.dma_start(x_res[:, slot, :], t["x_t"][x + 2]).then_inc(xr_in[slot], 16)
                sum_squares(r, OUT, x + 25)

            with pool.Fori(0, 7) as cc:
                for slot in range(2):
                    project(cc, slot)
            for slot in range(2):
                project(7, slot, more=False)
            pool.wait_ge(s.shift, 32)
            pool.wait_ge(s.ss_done, 4)
            pool.memset(acc[:, :], 0.0).then_inc(s.acc_zeroed, 1)
            pool.dma_start(g_fin[:, :], t["final_norm_g"].rearrange("(o n) -> o n", o=1).to_broadcast([P, D_MODEL])
                           ).then_inc(s.gf_in, 16)
            with pool.Fori(0, NCH) as c:
                with pool.Fori(0, FT) as f:
                    pool.wait_ge(s.silu_made, 4 * c + f + 1)
                    pool.tensor_tensor(t_a, t_a, rstd[:, 0:OUT], ALU.mult).then_inc(s.silu_scaled, 1)
            pool.wait_ge(s.acc_zeroed, 4)
            for x in range(KT - 1):
                pool.wait_ge(free[x % 2], 8 * (NCH - 1) + 31 + x // 2)
                sum_squares(res[:, x, :], OUT, x + 41)


def launch_arrays(inputs):
    inv = (np.float32(10000.0) ** (-np.arange(32, dtype=np.float32) / np.float32(32))).astype(np.float32)
    pos = np.concatenate([np.arange(N_META + SEQ), np.full(NB, PAST)]).astype(np.float32)
    ang = (pos[None, :] * inv[:, None]).astype(np.float32).astype(np.float64)
    c_cos = np.tile(np.cos(ang), (4, 1)).astype(np.float32)
    c_sin = np.concatenate([np.sin(ang), -np.sin(ang)] * 2).astype(np.float32)
    r, k = np.arange(P)[:, None], np.arange(2 * P)[None, :]
    band = (k >= r) & (k <= r + WINDOW)
    c_mask = np.stack([np.where(band & (k >= PADK), 0.0, -1e30), np.where(band, 0.0, -1e30)], 1).astype(np.float32)
    arrays = {n: np.ascontiguousarray(inputs[n]) for n in INS}
    arrays.update(c_cos=c_cos, c_sin=c_sin, c_mask=c_mask, c_ident=np.eye(P, dtype=np.float32))
    return arrays


INS = ["x_prompt", "x_sample", "cache_k", "cache_v", "state_conv", "meta_tokens", "norm1_g", "w_in", "conv_w",
       "conv_norm_g", "attn_norm_g", "attn_sinks", "w_out", "norm2_g", "w_gate", "w_up", "w_down", "final_norm_g"]
OUTS = {
    "y_prompt": (1, SEQ, D_MODEL),
    "y_sample": (NB, 1, D_MODEL),
    "new_k_prompt": (1, 1, WINDOW, N_KV, HEAD),
    "new_v_prompt": (1, 1, WINDOW, N_KV, HEAD),
    "new_conv_prompt": (1, 1, 2, CONV),
    "new_k_sample": (1, NB, WINDOW, N_KV, HEAD),
    "new_v_sample": (1, NB, WINDOW, N_KV, HEAD),
    "new_conv_sample": (1, NB, 2, CONV),
}


def kernel(**inputs):
    import concourse.bacc as bacc
    from concourse.bass_utils import run_bass_kernel_spmd

    nc = bacc.Bacc("TRN2", target_bir_lowering=False, num_devices=1)
    arrays = launch_arrays(inputs)
    t = {n: nc.dram_tensor(n, list(a.shape), F32, kind="ExternalInput").ap() for n, a in arrays.items()}
    for n, shape in OUTS.items():
        t[n] = nc.dram_tensor(n, list(shape), F32, kind="ExternalOutput").ap()
    t["x_t"] = nc.dram_tensor("x_t", [KT, P, OUT], F32).ap()
    build(nc, t)
    r = run_bass_kernel_spmd(nc, [arrays], core_ids=[0])
    return tuple(r.results[0][n] for n in OUTS)
```
